# Optimizing a Trainium2 kernel written in Bass

```python
import jax, jax.numpy as jnp
from jax import lax
import numpy as np

D_MODEL = 1024
BATCH = 1
SEQ = 512
DEPTH = 1

CONV_GROUPS = 8
ATTN_HEADS = 8
HEAD_DIM = D_MODEL // (CONV_GROUPS + ATTN_HEADS)
CONV_WIDTH = CONV_GROUPS * HEAD_DIM
ATTN_WIDTH = ATTN_HEADS * HEAD_DIM
MIX_WIDTH = CONV_WIDTH + ATTN_WIDTH
IN_WIDTH = 3 * CONV_WIDTH + 3 * ATTN_WIDTH
CONV_K = 3
MOBA_BLOCK = 256
MOBA_TOPK = 3
ATTN_Q_CHUNK = 64
PEER_HEADS = 8
PEER_NKEYS = 128
PEER_N_EXPERTS = PEER_NKEYS * PEER_NKEYS
PEER_DKEY = 256
PEER_TOPK = 16
PEER_TOKEN_CHUNK = 128
NORM_EPS = 1e-6
NEG_INF = -1e30

kernel_name = "hybrid_conv_moba_peer_block"

def rms_norm(x, gain):
    xf = x.astype(jnp.float32)
    y = xf * lax.rsqrt(jnp.mean(xf * xf, axis=-1, keepdims=True) + NORM_EPS)
    return (y * gain.astype(jnp.float32)).astype(x.dtype)

def group_rms_norm(y, gain):
    shp = y.shape
    yg = y.reshape(shp[:-1] + (shp[-1] // HEAD_DIM, HEAD_DIM)).astype(jnp.float32)
    yg = yg * lax.rsqrt(jnp.mean(yg * yg, axis=-1, keepdims=True) + NORM_EPS)
    return (yg.reshape(shp) * gain.astype(jnp.float32)).astype(y.dtype)

def causal_depthwise_conv(u, w):
    C = u.shape[-1]
    rhs = w[:, None, :].astype(u.dtype)
    return lax.conv_general_dilated(u, rhs, window_strides=(1,), padding=[(CONV_K - 1, 0)],
                                    dimension_numbers=("NWC", "WIO", "NWC"),
                                    feature_group_count=C)

def gather_blocks(blocks, idx):
    return jax.vmap(jax.vmap(lambda t, i: t[i]))(blocks, idx)

def moba_attention(q, k, v):
    B, S, H, dh = q.shape
    nb = -(-S // MOBA_BLOCK)
    pad = nb * MOBA_BLOCK - S
    scale = dh ** -0.5
    qh = q.transpose(0, 2, 1, 3)
    kh = jnp.pad(k.transpose(0, 2, 1, 3), ((0, 0), (0, 0), (0, pad), (0, 0)))
    vh = jnp.pad(v.transpose(0, 2, 1, 3), ((0, 0), (0, 0), (0, pad), (0, 0)))
    kb = kh.reshape(B, H, nb, MOBA_BLOCK, dh)
    vb = vh.reshape(B, H, nb, MOBA_BLOCK, dh)
    qblk = jnp.arange(S) // MOBA_BLOCK
    n_sel = min(MOBA_TOPK, nb - 1)
    nc = S // ATTN_Q_CHUNK
    q_c = qh.reshape(B, H, nc, ATTN_Q_CHUNK, dh).transpose(2, 0, 1, 3, 4)
    xs = (jnp.arange(nc), q_c)
    if n_sel > 0:
        kmean = jnp.mean(kb.astype(jnp.float32), axis=3)
        gate = jnp.einsum("bhsd,bhnd->bhsn", qh.astype(jnp.float32), kmean)
        past = jnp.arange(nb)[None, :] < qblk[:, None]
        gate = jnp.where(past, gate, NEG_INF)
        _, sel = lax.top_k(gate, n_sel)
        valid = sel < qblk[:, None]
        sel_c = sel.reshape(B, H, nc, ATTN_Q_CHUNK, n_sel).transpose(2, 0, 1, 3, 4)
        valid_c = valid.reshape(B, H, nc, ATTN_Q_CHUNK, n_sel).transpose(2, 0, 1, 3, 4)
        xs = xs + (sel_c, valid_c)

    def chunk(args):
        ci, qc = args[0], args[1]
        q0 = ci * ATTN_Q_CHUNK
        blk = q0 // MOBA_BLOCK
        k_own = lax.dynamic_index_in_dim(kb, blk, axis=2, keepdims=False)
        v_own = lax.dynamic_index_in_dim(vb, blk, axis=2, keepdims=False)
        qpos = q0 + jnp.arange(ATTN_Q_CHUNK)
        kpos = blk * MOBA_BLOCK + jnp.arange(MOBA_BLOCK)
        own_mask = kpos[None, :] <= qpos[:, None]
        s_own = jnp.einsum("bhqd,bhkd->bhqk", qc, k_own,
                           preferred_element_type=jnp.float32) * scale
        s_own = jnp.where(own_mask, s_own, NEG_INF)
        if n_sel == 0:
            p_own = jax.nn.softmax(s_own, axis=-1).astype(v_own.dtype)
            return jnp.einsum("bhqk,bhkd->bhqd", p_own, v_own)
        selc, validc = args[2], args[3]
        k_sel = gather_blocks(kb, selc)
        v_sel = gather_blocks(vb, selc)
        s_sel = jnp.einsum("bhqd,bhqnkd->bhqnk", qc, k_sel,
                           preferred_element_type=jnp.float32) * scale
        s_sel = jnp.where(validc[..., None], s_sel, NEG_INF)
        n_past = n_sel * MOBA_BLOCK
        s_all = jnp.concatenate([s_sel.reshape(s_sel.shape[:3] + (n_past,)), s_own], axis=-1)
        p = jax.nn.softmax(s_all, axis=-1).astype(v_own.dtype)
        p_sel = p[..., :n_past].reshape(s_sel.shape)
        p_own = p[..., n_past:]
        return (jnp.einsum("bhqnk,bhqnkd->bhqd", p_sel, v_sel)
                + jnp.einsum("bhqk,bhkd->bhqd", p_own, v_own))

    out = lax.map(chunk, xs)
    return out.transpose(1, 0, 3, 2, 4).reshape(B, S, H * dh)

def hybrid_mixer(h, w_in, conv_w, group_gain, w_out):
    B, S, _ = h.shape
    p = h @ w_in
    cuts = [CONV_WIDTH, 2 * CONV_WIDTH, 3 * CONV_WIDTH,
            3 * CONV_WIDTH + ATTN_WIDTH, 3 * CONV_WIDTH + 2 * ATTN_WIDTH]
    gb, gc, hx, q, k, v = jnp.split(p, cuts, axis=-1)
    y_conv = gb * causal_depthwise_conv(gc * hx, conv_w)
    shp = (B, S, ATTN_HEADS, HEAD_DIM)
    y_attn = moba_attention(q.reshape(shp), k.reshape(shp), v.reshape(shp))
    y = group_rms_norm(jnp.concatenate([y_conv, y_attn], axis=-1), group_gain)
    return y @ w_out

def peer_ffn(h, w_pq, sub_keys, u, v):
    B, S, D = h.shape
    T = B * S
    ht = h.reshape(T, D)
    q = (ht @ w_pq).reshape(T, PEER_HEADS, 2, PEER_DKEY // 2)
    s = jnp.einsum("thpd,hpnd->thpn", q, sub_keys,
                   preferred_element_type=jnp.float32)
    s1, i1 = lax.top_k(s[:, :, 0], PEER_TOPK)
    s2, i2 = lax.top_k(s[:, :, 1], PEER_TOPK)
    cand_s = (s1[..., :, None] + s2[..., None, :]).reshape(T, PEER_HEADS, PEER_TOPK * PEER_TOPK)
    cand_i = (i1[..., :, None] * PEER_NKEYS + i2[..., None, :]).reshape(T, PEER_HEADS, PEER_TOPK * PEER_TOPK)
    top_s, pos = lax.top_k(cand_s, PEER_TOPK)
    eidx = jnp.take_along_axis(cand_i, pos, axis=-1)
    g = jax.nn.softmax(top_s, axis=-1)
    nc = T // PEER_TOKEN_CHUNK

    def chunk(args):
        xc, ec, gcw = args
        a = jnp.einsum("td,thkd->thk", xc, u[ec])
        w = (gcw * jax.nn.gelu(a.astype(jnp.float32))).astype(xc.dtype)
        return jnp.einsum("thk,thkd->td", w, v[ec])

    y = lax.map(chunk, (ht.reshape(nc, PEER_TOKEN_CHUNK, D),
                        eidx.reshape(nc, PEER_TOKEN_CHUNK, PEER_HEADS, PEER_TOPK),
                        g.reshape(nc, PEER_TOKEN_CHUNK, PEER_HEADS, PEER_TOPK)))
    return y.reshape(B, S, D)

def setup_inputs(seed: int = 0) -> dict:
    key = jax.random.key(seed)
    ks = jax.random.split(key, 16)
    D = D_MODEL

    def nrm(k, shape, scale):
        return jax.random.normal(k, shape, jnp.float32) * scale

    return {
        "x": nrm(ks[0], (BATCH, SEQ, D), 1.0),
        "c": nrm(ks[1], (BATCH, D), 1.0),
        "ada_w": nrm(ks[2], (DEPTH, D, 6 * D), 0.5 * D ** -0.5),
        "ada_b": nrm(ks[3], (DEPTH, 6 * D), 0.02),
        "mix_pre_gain": 1.0 + nrm(ks[4], (DEPTH, D), 0.02),
        "mix_post_gain": 1.0 + nrm(ks[5], (DEPTH, D), 0.02),
        "w_in": nrm(ks[6], (DEPTH, D, IN_WIDTH), D ** -0.5),
        "conv_w": nrm(ks[7], (DEPTH, CONV_K, CONV_WIDTH), CONV_K ** -0.5),
        "group_gain": 1.0 + nrm(ks[8], (DEPTH, MIX_WIDTH), 0.02),
        "w_out": nrm(ks[9], (DEPTH, MIX_WIDTH, D), MIX_WIDTH ** -0.5),
        "ffn_pre_gain": 1.0 + nrm(ks[10], (DEPTH, D), 0.02),
        "ffn_post_gain": 1.0 + nrm(ks[11], (DEPTH, D), 0.02),
        "peer_wq": nrm(ks[12], (DEPTH, D, PEER_HEADS * PEER_DKEY), D ** -0.5),
        "peer_keys": nrm(ks[13], (DEPTH, PEER_HEADS, 2, PEER_NKEYS, PEER_DKEY // 2), (PEER_DKEY // 2) ** -0.5),
        "peer_u": nrm(ks[14], (DEPTH, PEER_N_EXPERTS, D), D ** -0.5),
        "peer_v": nrm(ks[15], (DEPTH, PEER_N_EXPERTS, D), D ** -0.5),
    }

def reference(x, c, ada_w, ada_b, mix_pre_gain, mix_post_gain, w_in, conv_w, group_gain, w_out,
              ffn_pre_gain, ffn_post_gain, peer_wq, peer_keys, peer_u, peer_v):
    for l in range(DEPTH):
        mod = (jax.nn.silu(c) @ ada_w[l] + ada_b[l])[:, None, :]
        sh1, sc1, g1, sh2, sc2, g2 = jnp.split(mod, 6, axis=-1)
        h = rms_norm(x, mix_pre_gain[l]) * (1.0 + sc1) + sh1
        y = hybrid_mixer(h, w_in[l], conv_w[l], group_gain[l], w_out[l])
        x = x + g1 * rms_norm(y, mix_post_gain[l])
        h = rms_norm(x, ffn_pre_gain[l]) * (1.0 + sc2) + sh2
        y = peer_ffn(h, peer_wq[l], peer_keys[l], peer_u[l], peer_v[l])
        x = x + g2 * rms_norm(y, ffn_post_gain[l])
    return x


_drawn_inputs = setup_inputs


def setup_inputs(seed=0):
    import zlib

    import numpy as np

    out = dict(_drawn_inputs(seed))
    spreads = {}
    factors = {}
    for name, (base, spread) in spreads.items():
        noise = np.random.default_rng([zlib.crc32(name.encode()), seed]).standard_normal(out[name].shape)
        drawn = base * np.exp(spread * noise) if base else spread * noise
        out[name] = __import__('jax').numpy.asarray(drawn.astype(out[name].dtype))
    for name, factor in factors.items():
        out[name] = (out[name] * factor).astype(out[name].dtype)
    return out
```

```python
from contextlib import ExitStack

import numpy as np

import concourse.bass as bass
from concourse import mybir
from concourse.alu_op_type import AluOpType as ALU

ACT = mybir.ActivationFunctionType
F32 = mybir.dt.float32
F16 = mybir.dt.float16
BF16 = mybir.dt.bfloat16
U32 = mybir.dt.uint32
AX = mybir.AxisListType

P = 128
D = 1024
T = 512
KC = D // P
TT = T // P
HD = 64
NCONV = 4
NHEAD = 8
PH = 8
NK = 128
K16 = 16
NE = NK
EPS = 1e-6
NEG = -1e30

W_SCALE = 256.0
G_SCALE = 64.0
UNSCALE = 1.0 / W_SCALE
Y_UNSCALE = 1.0 / (W_SCALE * G_SCALE)

PG1, PG1P, PGG, PG2, PG2P, PC_, PB, PCW = 0, 8, 16, 24, 32, 40, 48, 96
NPAR = 96 + 3 * NCONV

SH1, SC1, GT1, SH2, SC2, GT2 = (8 * j for j in range(6))

WIN_ORDER = list(range(12, 24)) + list(range(4, 12)) + list(range(0, 4))
PAIRS = [("ada", 2 * j) for j in range(8)]
for _j in range(12):
    PAIRS += [("win", 2 * _j), ("ada", 16 + 2 * _j)]
for _j in range(4):
    PAIRS += [("wout", 2 * _j), ("ada", 40 + 2 * _j)]
WQ_PAIR0 = len(PAIRS)
U_PAIR0 = WQ_PAIR0 + 8
V_PAIR0 = U_PAIR0 + NE // 2
SLOTS = 4
RING = 4
SPLIT0 = {"win": 0, "wout": 24, "wq": 32, "u": 48, "v": 48 + NE}
PAIR_AT = {p: n for n, p in enumerate(PAIRS)}
ADA_SEEN = {}
_n = 0
for _p, (_kind, _i) in enumerate(PAIRS):
    if _kind == "ada":
        _n += 2
        ADA_SEEN[_p] = _n

UNITS = TT * PH
GTOK = 8
GCH = T // GTOK
G0 = UNITS + 8
GBLK = 64
NV_S0 = SPLIT0["v"]


class Chain:

    def __init__(self, eng, sem):
        self.eng, self.sem, self.base, self.n = eng, sem, 0, 0

    def link(self, ins):
        self.n += 1
        ins.then_inc(self.sem, 1)
        self.eng.wait_ge(self.sem, self.base + self.n)

    def enter(self, it, steps):
        self.start, self.base, self.n = self.n, it * steps + self.n, 0

    def leave(self, steps, times):
        assert self.n == steps, (self.n, steps)
        self.base, self.n = 0, self.start + steps * times


def build(nc, xT, par, ada, win, wout, wq, keys, u, v, out):
    a_dram = nc.dram_tensor("act_spill", (NE, P, T), F32, kind="Internal").ap()
    g_dram = nc.dram_tensor("gate_spill", (T // GBLK, P, NK, GBLK), F32, kind="Internal").ap()
    with ExitStack() as ctx:
        def sb(name, shape, dt=F32):
            return ctx.enter_context(nc.sbuf_tensor(name, shape, dt))

        def sem(name):
            return ctx.enter_context(nc.semaphore(name))

        bank = [ctx.enter_context(nc.psum_tensor(f"bank{b}", [P, 512], F32)) for b in range(8)]

        stage = sb("stage", [P, SLOTS, 2, 1024])
        w_hi = sb("w_hi", [P, RING, KC, P], F16)
        w_lo = sb("w_lo", [P, RING, KC, P], F16)
        x_sb = sb("x_sb", [P, KC, T])
        act_hi = sb("act_hi", [P, KC, T], F16)
        act_lo = sb("act_lo", [P, KC, T], F16)
        y_sb = sb("y_sb", [P, KC, T])
        big = sb("big", [P, 16384])
        par_sb = sb("par_sb", [P, NPAR])
        mod = sb("mod", [P, 48])
        amul = sb("amul", [P, 2, KC])
        gmul = sb("gmul", [P, 2, KC])
        silu_c = sb("silu_c", [P, KC])
        norm_tmp = sb("norm_tmp", [P, 6, T])
        rstd, sq, tmp = (norm_tmp[:, 2 * j:2 * j + 2, :] for j in range(3))
        a_out = norm_tmp[:, 2:6, :]
        ones = sb("ones", [P, P])
        group_ones = sb("group_ones", [P, P])
        ident = sb("ident", [P, P])
        ident_bf = sb("ident_bf", [P, P], BF16)
        mask_bf = sb("mask_bf", [P, P], BF16)
        iota_f = sb("iota_f", [P, P], F16)
        iota16 = sb("iota16", [P, K16])
        eps_sb = sb("eps_sb", [P, 1])
        keys_sb = sb("keys_sb", [P, 2 * PH, NK])
        pq = sb("pq", [P, 2, T])

        def carve(at, shape):
            n = int(np.prod(shape))
            v_ = big[:, at:at + n]
            names = " ".join(f"a{j}" for j in range(len(shape)))
            if len(shape) > 1:
                v_ = v_.rearrange(f"p ({names}) -> p {names}", **{f"a{j}": s for j, s in enumerate(shape)})
            return v_, at + n

        at = 0
        qT, at = carve(at, (4, T))
        kT, at = carve(at, (4, T))
        vT, at = carve(at, (2, T))
        v_tok, at = carve(at, (TT, 512))
        gcT, at = carve(at, (4, T))
        conv_in, at = carve(at, (4, T + 2))
        probs, at = carve(at, (2, T))
        probsT, at = carve(at, (2, T))
        assert at <= 16384
        gate_buf, _ = carve(0, (2, NK, GBLK))
        at = 0
        a_in, at = carve(at, (4, T))
        g_in, at = carve(at, (4, T))
        wgt, at = carve(at, (2, T))
        wgt_hi = big[:, at:at + 4 * T // 2].bitcast(F16).rearrange("p (r t) -> p r t", r=4)
        at += 4 * T // 2
        wgt_lo = big[:, at:at + 4 * T // 2].bitcast(F16).rearrange("p (r t) -> p r t", r=4)
        at += 4 * T // 2
        y_f, at = carve(at, (KC, T))
        assert at <= 16384

        negmax = sb("negmax", [P, 2])
        psum_row = sb("psum_row", [P, 2])
        rrow = sb("rrow", [P, 2])
        top_v = sb("top_v", [P, TT, K16])
        top_i = sb("top_i", [P, TT, K16], U32)
        work1 = sb("work1", [P, TT, NK])
        all_v = sb("all_v", [P, TT, 2 * PH, K16])
        all_i = sb("all_i", [P, TT, 2 * PH, K16])
        cand = sb("cand", [P, 256])
        cand2 = sb("cand2", [P, 256])
        best_v = sb("best_v", [P, K16])
        best_p = sb("best_p", [P, K16], U32)
        zeros16 = sb("zeros16", [P, P], F16)
        rank = sb("rank", [P, 2, 2, K16], U32)
        onehot16 = sb("onehot16", [P, 2, 2, 256])
        sel_i = y_sb[:, 6:8, :]
        sel_v = sb("sel_v", [P, UNITS * K16])
        sel_sum = sb("sel_sum", [P, UNITS])
        idxT = keys_sb[:, :, :].rearrange("p h n -> p (h n)").rearrange("p (a t) -> p a t", a=4)
        gateT = pq[:, 0, :]
        gate16 = pq[:, 1, 0:T // 2].bitcast(F16)
        scal = sb("scal", [P, 2, 4, GTOK])
        oh = y_sb[:, :, :].rearrange("p a b -> p (a b)").bitcast(F16)
        oh_b = oh[:, 0:2048].rearrange("p (r t n) -> p r t n", r=2, t=GTOK)
        oh_h = oh[:, 2048:4096].rearrange("p (r t n) -> p r t n", r=2, t=GTOK)
        oh_l = oh[:, 4096:6144].rearrange("p (r t n) -> p r t n", r=2, t=GTOK)

        s_par = sem("params_in")
        s_x = sem("x_in")
        s_keys = sem("keys_in")
        s_stage = [sem(f"stage_in{j}") for j in range(SLOTS)]
        s_const = sem("consts_ready")
        s_hi = sem("hi_ready")
        s_lo = sem("lo_ready")
        s_tile = sem("tile_done")
        s_evac = [sem(f"tile_evacuated{j}") for j in range(2)]
        s_silu = sem("silu_ready")
        s_ada = sem("ada_used")
        s_mod = sem("mod_ready")
        s_sq = sem("squares_ready")
        s_stat = sem("squares_summed")
        s_root = sem("root_ready")
        s_rstd = sem("rstd_ready")
        s_rused = sem("rstd_used")
        s_xr = sem("x_rstd_ready")
        s_act32 = sem("act32_ready")
        s_acthi = sem("act_hi_ready")
        s_actlo = sem("act_lo_ready")
        s_qk = sem("qkv_ready")
        s_vtr = sem("v_transposed")
        s_vtok = sem("v_tok_ready")
        s_score = sem("scores_ready")
        s_nmax = sem("negmax_ready")
        s_exp = sem("exp_ready")
        s_norm = sem("probs_ready")
        s_ptr = sem("probs_transposed")
        s_pT = sem("probsT_ready")
        s_pv = sem("pv_done")
        s_ya = sem("attn_out_ready")
        s_yc = sem("conv_out_ready")
        s_gc = sem("gc_ready")
        s_yw = sem("mixer_out_ready")
        s_x1 = sem("x1_ready")
        s_pq = sem("peer_q_ready")
        s_ps = [sem(f"peer_scores_ready{j}") for j in range(2)]
        s_psr = [sem(f"peer_scores_read{j}") for j in range(2)]
        s_rank = sem("rank_ready")
        s_oh = sem("onehot_index_ready")
        s_seli = sem("sel_i_ready")
        s_pool = sem("pool_step")
        s_selv = sem("sel_v_ready")
        s_selexp = sem("sel_exp_ready")
        s_gate = sem("gate_ready")
        s_gtr = sem("gate_transposed")
        s_idx = sem("idxT_ready")
        s_scal = sem("scalars_ready")
        s_ohb = sem("oh_b_ready")
        s_oha = [sem(f"oh_a_ready{j}") for j in range(2)]
        s_gb = [sem(f"gate_bank_ready{j}") for j in range(2)]
        s_gev = [sem(f"gates_evacuated{j}") for j in range(2)]
        s_gout = [sem(f"gates_out{j}") for j in range(2)]
        s_gelu = sem("gelu_ready")
        s_aout = [sem(f"act_out{j}") for j in range(4)]
        s_agin = [sem(f"act_gate_in{j}") for j in range(4)]
        s_w32 = sem("weighted_ready")
        s_whi = sem("weighted_hi_ready")
        s_wlo = sem("weighted_lo_ready")
        s_ysum = sem("y_summed")
        s_fin0 = sem("y_first_evacuated")
        s_fin = sem("y_odd_evacuated")
        s_fin2 = sem("out_ready")
        s_out = sem("out_stored")
        s_dve = sem("dve_chain")
        s_act = sem("act_chain")
        s_apart = sem("waits_apart")

        PRIMED = 1

        block = ctx.enter_context(nc.Block())

        def apart(eng):
            eng.sem_inc(s_apart, 1)

        def landed(eng, kind, i):
            p = PAIR_AT[(kind, i - i % 2)]
            eng.wait_ge(s_stage[p % SLOTS], 16 * (p // SLOTS + 1))
            return stage[:, p % SLOTS, i % 2, :]

        def landed8(eng, pair0, it, j):
            eng.wait_ge(s_stage[j // 2 % SLOTS], it * 16 + 16 * (pair0 // SLOTS + j // 8 + 1))
            return stage[:, j // 2 % SLOTS, j % 2, :]

        @block.sync
        def _(sp):
            sp.dma_start(par_sb[:, :], par).then_inc(s_par, 16)
            sp.dma_start(x_sb[:, :, :], xT).then_inc(s_x, 16)
            src = {"ada": ada, "win": win, "wout": wout}

            def load_pair(slot, chunks):
                sp.dma_start(stage[:, slot, :, :], chunks.rearrange("n p f -> p n f")).then_inc(s_stage[slot], 16)

            def freed(p):
                kind, i = PAIRS[p]
                if kind == "ada":
                    sp.wait_ge(s_ada, ADA_SEEN[p])
                else:
                    sp.wait_ge(s_lo, SPLIT0[kind] + i + 2)

            for p, (kind, i) in enumerate(PAIRS):
                if p >= SLOTS:
                    freed(p - SLOTS)
                j = WIN_ORDER[i] if kind == "win" else i
                load_pair(p % SLOTS, src[kind][j:j + 2])
                if p == 20:
                    sp.dma_start(keys_sb[:, :, :], keys).then_inc(s_keys, 16)
            for s in range(SLOTS):
                freed(WQ_PAIR0 - SLOTS + s)
                load_pair(s, wq[2 * s:2 * s + 2])

            def load_next(w, row, s0, s):
                sp.wait_ge(s_lo, s0 + 2 * s + 2)
                load_pair(s, w[bass.ds(row + 2 * s, 2)])

            for s in range(SLOTS):
                load_next(wq, 8, SPLIT0["wq"], s)
            for s in range(SLOTS):
                load_next(u, 0, SPLIT0["wq"] + 8, s)

            def spill_a(c, j):
                sp.wait_ge(s_gelu, c + 1)
                sp.dma_start(a_dram[bass.ds(c, 1)].rearrange("n p t -> p (n t)"),
                             a_out[:, j, :]).then_inc(s_aout[j], 16)

            def group(it, after, row):
                for half in range(2):
                    for s in (2 * half, 2 * half + 1):
                        load_next(after, row, it * 8 + SPLIT0["u"], s)
                    for j in range(4):
                        spill_a(it * 8 + 4 * half + j, j)

            def store_gates(blk, b):
                for r in range(2):
                    sp.wait_ge(s_gev[r], blk * 8 + 8 + PRIMED)
                sp.dma_start(g_dram[bass.ds(blk, 1)].rearrange("n p i t -> p (n i t)"),
                             gate_buf[:, b, :, :].rearrange("p i t -> p (i t)")).then_inc(s_gout[b], 16)

            with sp.Fori(0, G0 // 8) as it:
                group(it, u, it * 8 + 8)
            with sp.Fori(0, T // GBLK // 2) as it:
                for b in range(2):
                    group(it * 2 + (G0 // 8 + b), u, it * 16 + (G0 + 8 * b + 8))
                    store_gates(it * 2 + b, b)
            with sp.Fori((G0 + GCH) // 8, NE // 8 - 1) as it:
                group(it, u, it * 8 + 8)
            group(NE // 8 - 1, v, 0)
            for j in range(4):
                sp.wait_ge(s_aout[j], 16 * (NE // 4))
            for b in range(2):
                sp.wait_ge(s_gout[b], 16 * (T // GBLK // 2))

            def load_ag(c, j):
                sp.dma_start(a_in[:, j, :], a_dram[bass.ds(c, 1)].rearrange("n p t -> p (n t)")
                             ).then_inc(s_agin[j], 16)
                sp.dma_start(g_in[:, j, :].rearrange("p (b t) -> p b t", b=T // GBLK),
                             g_dram[:, :, bass.ds(c, 1), :].rearrange("b p i t -> p b (i t)")
                             ).then_inc(s_agin[j], 16)

            def v_group(it, last):
                for half in range(2):
                    if not last:
                        for s in (2 * half, 2 * half + 1):
                            load_next(v, it * 8 + 8, it * 8 + SPLIT0["v"], s)
                    if not (last and half):
                        for j in range(4):
                            sp.wait_ge(s_w32, it * 8 + 4 * half + j + 1)
                            load_ag(it * 8 + 4 * half + 4 + j, j)

            for j in range(4):
                load_ag(j, j)
            with sp.Fori(0, NE // 8 - 1) as it:
                v_group(it, False)
            v_group(NE // 8 - 1, True)
            for kc in range(KC):
                sp.wait_ge(s_fin2, kc + 1)
                sp.dma_start(out[:, kc, :], y_f[:, kc, :]).then_inc(s_out, 16)
            sp.wait_ge(s_out, 16 * KC)

        @block.gpsimd
        def _(pool):
            ch = Chain(pool, s_pool)
            ch.link(pool.memset(ones[:, :], 1.0))
            ch.link(pool.memset(zeros16[:, :], 0.0))
            ch.link(pool.memset(ident[:, :], 0.0))
            ch.link(pool.memset(mask_bf[:, :], 0.0))
            ch.link(pool.memset(group_ones[:, :], 0.0))
            ch.link(pool.memset(eps_sb[:, :], EPS))
            ch.link(pool.memset(group_ones[0:HD, 0:HD], 1.0))
            ch.link(pool.memset(group_ones[HD:P, HD:P], 1.0))
            ch.link(pool.affine_select(out=ident[:, :], in_=ident[:, :], compare_op=ALU.not_equal, fill=1.0,
                                       base=0, pattern=[[-1, P]], channel_multiplier=1))
            ch.link(pool.affine_select(out=mask_bf[:, :], in_=mask_bf[:, :], compare_op=ALU.is_ge, fill=NEG,
                                       base=0, pattern=[[-1, P]], channel_multiplier=1))
            ch.link(pool.tensor_copy(ident_bf[:, :], ident[:, :]))
            ch.link(pool.iota(iota_f[:, :], pattern=[[1, P]], base=0, channel_multiplier=0,
                              allow_small_or_imprecise_dtypes=True))
            ch.link(pool.iota(iota16[:, :], pattern=[[1, K16]], base=0, channel_multiplier=0,
                              allow_small_or_imprecise_dtypes=True))
            pool.memset(conv_in[:, :, 0:2], 0.0).then_inc(s_const, 1)

            for part, tiles in ((0, 0), (1, 24), (2, 32)):
                if tiles:
                    pool.wait_ge(s_tile, tiles)
                for kc in range(KC):
                    m = KC * part + kc
                    pool.wait_ge(s_act32, m + 1)
                    pool.tensor_copy(act_hi[:, kc, :], tmp[:, m % 2, :]).then_inc(s_acthi, 1)

            key_rows = all_i[:, :, :, :].rearrange("p t h k -> p (t h) k")
            with pool.Fori(0, UNITS // 2) as it:
                for r in range(2):
                    pool.wait_ge(s_rank, it * 2 + r + 1)
                    hot = onehot16[:, r, :, :].rearrange("p h (k a) -> p h k a", k=K16)
                    pool.tensor_tensor(
                        out=hot, in0=hot,
                        in1=key_rows[:, bass.ds(it * 4 + 2 * r, 2), :].unsqueeze(2).to_broadcast([P, 2, K16, K16]),
                        op=ALU.mult).then_inc(s_oh, 1)
            pool.wait_ge(s_idx, 1)
            with pool.Fori(0, GCH // 2) as it:
                for r in range(2):
                    pool.wait_ge(s_oha[r], it + PRIMED)
                    pool.wait_ge(s_gb[r], it * 2 + PRIMED)
                    pool.tensor_copy(scal[:, r, :, :], idxT[:, :, bass.ds(it * (2 * GTOK) + GTOK * r, GTOK)]
                                     ).then_inc(s_scal, 1)
                    pool.wait_ge(s_scal, it * 2 + r + 1)
                    apart(pool)
                    for t in range(GTOK):
                        ins = pool.tensor_scalar(oh_b[:, r, t, :], iota_f[:, :], scal[:, r, 1, t:t + 1], None,
                                                 ALU.is_equal)
                    ins.then_inc(s_ohb, 1)

        @block.scalar
        def _(act):
            ch = Chain(act, s_act)

            def hi(s, piece):
                act.activation(w_hi[:, s % RING, :, :].rearrange("p a b -> p (a b)"), piece, ACT.Copy,
                               scale=W_SCALE).then_inc(s_hi, 1)

            def hi_at(s):
                if s < SPLIT0["wq"]:
                    kind = "win" if s < SPLIT0["wout"] else "wout"
                    piece = landed(act, kind, s - SPLIT0[kind])
                else:
                    piece = landed8(act, WQ_PAIR0, 0, s - SPLIT0["wq"])
                if s >= RING:
                    act.wait_ge(s_tile, s - RING + 1)
                hi(s, piece)

            def square(m, src):
                if m >= 2:
                    act.wait_ge(s_stat, m - 1)
                act.activation(sq[:, m % 2, :], src, ACT.Square).then_inc(s_sq, 1)

            def root(r, m, src, width):
                act.wait_ge(s_stat, m + 1)
                if r >= 2:
                    act.wait_ge(s_rused, r - 1)
                act.activation(rstd[:, r % 2, :], src, ACT.Sqrt, bias=eps_sb[:, :],
                               scale=1.0 / width).then_inc(s_root, 1)

            def scale_shift(which, shift, part):
                for kc in range(KC):
                    act.wait_ge(s_xr, KC * which + kc + 1)
                    act.activation(tmp[:, kc % 2, :], tmp[:, kc % 2, :], ACT.Identity,
                                   bias=mod[:, shift + kc:shift + kc + 1],
                                   scale=amul[:, which, kc:kc + 1]).then_inc(s_act32, 1)

            for r in range(2):
                act.sem_inc(s_gev[r], PRIMED)
            act.wait_ge(s_par, 16)
            act.activation(silu_c[:, :], par_sb[:, PC_:PC_ + KC], ACT.Silu).then_inc(s_silu, 1)
            act.wait_ge(s_x, 16)
            act.wait_ge(s_const, 1)
            for kc in range(KC):
                square(kc, x_sb[:, kc, :])
            root(0, KC - 1, bank[6][:, :], D)
            act.wait_ge(s_mod, 1)
            scale_shift(0, SH1, 0)
            for s in range(RING):
                hi_at(s)
            for i in range(12):
                act.wait_ge(s_tile, i + 1)
                src = bank[i % 2][:, :]
                if i < 4:
                    ins = act.activation(qT[:, i, :], src, ACT.Copy, scale=UNSCALE * HD ** -0.5)
                elif i < 8:
                    ins = act.activation(kT[:, i - 4, :], src, ACT.Copy, scale=UNSCALE)
                else:
                    if i >= 10:
                        act.wait_ge(s_vtr, i - 9)
                    ins = act.activation(vT[:, i % 2, :], src, ACT.Copy, scale=UNSCALE)
                ins.then_inc(s_evac[i % 2], 1)
                hi_at(i + RING)
            for k in range(36):
                if k < UNITS:
                    n, b = k, k % 2
                    w = P * (n % TT + 1)
                    act.wait_ge(s_nmax, n + 1)
                    if n >= 2:
                        act.wait_ge(s_ptr, n - 1)
                    act.activation(probs[:, b, 0:w], bank[2 + b][:, 0:w], ACT.Exp, bias=negmax[:, b:b + 1],
                                   accum_out=psum_row[:, b:b + 1]).then_inc(s_exp, 1)
                if 1 <= k <= UNITS:
                    n, b = k - 1, (k - 1) % 2
                    w = P * (n % TT + 1)
                    act.wait_ge(s_ptr, n + 1)
                    if n >= 2:
                        act.wait_ge(s_pv, n - 1)
                    act.activation(probsT[:, b, 0:w], bank[4 + b][:, 0:w], ACT.Copy).then_inc(s_pT, 1)
                if k % 3 == 2:
                    i = 12 + k // 3
                    if i < 16:
                        act.wait_ge(s_tile, i + 1)
                        act.activation(gcT[:, i - 12, :], bank[i % 2][:, :], ACT.Copy,
                                       scale=UNSCALE).then_inc(s_evac[i % 2], 1)
                    hi_at(i + RING)
                if k >= 9 and (k - 9) % 8 == 0:
                    pair = (k - 9) // 8
                    act.wait_ge(s_pv, 8 * pair + 8)
                    act.activation(y_sb[:, NCONV + pair, :], bank[6][:, :], ACT.Copy).then_inc(s_ya, 1)
            act.wait_ge(s_ya, 4)
            act.wait_ge(s_yc, 4)
            for j in range(KC + 1):
                if j < KC:
                    square(KC + j, y_sb[:, j, :])
                if j:
                    root(j, KC + j - 1, bank[2 + (j - 1) % 2][:, :], HD)
            for i in range(KC):
                act.wait_ge(s_tile, 24 + i + 1)
                act.activation(y_sb[:, i, :], bank[i % 2][:, :], ACT.Copy, scale=UNSCALE
                               ).then_inc(s_evac[i % 2], 1)
                act.wait_ge(s_evac[i % 2], (24 + i) // 2 + 1)
                square(2 * KC + i, y_sb[:, i, :])
                hi_at(24 + i + RING)
            root(9, 3 * KC - 1, bank[5][:, :], D)
            for kc in range(KC):
                act.wait_ge(s_x1, kc + 1)
                square(3 * KC + kc, x_sb[:, kc, :])
            root(10, 4 * KC - 1, bank[6][:, :], D)
            act.wait_ge(s_mod, 2)
            scale_shift(1, SH2, 2)
            with act.Fori(0, 2) as it:
                for j in range(8):
                    act.wait_ge(s_tile, it * 8 + 32 + j + 1)
                    act.wait_ge(s_ps[j % 2], it * 4 + j // 2 + PRIMED)
                    act.activation(pq[:, j % 2, :], bank[j % 2][:, :], ACT.Copy, scale=UNSCALE
                                   ).then_inc(s_evac[j % 2], 1)
                    hi(32 + j + RING, landed8(act, WQ_PAIR0, it, j + RING))

            def gelu(c, it, j, first=False):
                act.wait_ge(s_tile, c + SPLIT0["u"] + 1)
                if not (first and j < 4):
                    act.wait_ge(s_aout[j % 4], it * 32 + 16 * (j // 4))
                act.activation(a_out[:, j % 4, :], bank[j % 2][:, :], ACT.Gelu_apprx_tanh,
                               scale=UNSCALE).then_inc(s_gelu, 1)
                hi(j, landed8(act, U_PAIR0, it, j + RING))

            for j in range(8):
                gelu(j, 0, j, first=True)
            with act.Fori(1, UNITS // 8) as it:
                for j in range(8):
                    gelu(it * 8 + j, it, j)
            act.wait_ge(s_selv, 1)
            act.activation(sel_v[:, :], sel_v[:, :], ACT.Exp).then_inc(s_selexp, 1)
            for j in range(8):
                gelu(UNITS + j, UNITS // 8, j)

            def gate_buffers(it, first):
                for b in range(2):
                    if not first:
                        act.wait_ge(s_gout[b], it * 16)
                    for j in range(8):
                        gelu(it * 16 + (G0 + 8 * b + j), it * 2 + (G0 // 8 + b), j)
                        for q in range(2):
                            act.wait_ge(s_gb[j % 2], it * 16 + 8 * b + 2 * (j // 2) + q + 1 + PRIMED)
                            act.activation(gate_buf[:, b, :, GTOK * j + 4 * q:GTOK * j + 4 * q + 4],
                                           bank[2 + 2 * (j % 2) + q][:, :].rearrange("p (t i) -> p i t", t=4),
                                           ACT.Copy).then_inc(s_gev[j % 2], 1)

            gate_buffers(0, True)
            with act.Fori(1, T // GBLK // 2) as it:
                gate_buffers(it, False)
            with act.Fori((G0 + GCH) // 8, NE // 8) as it:
                for j in range(8):
                    gelu(it * 8 + j, it, j)

            def w_high(c, j):
                act.wait_ge(s_w32, c + 1)
                act.activation(wgt_hi[:, j % 4, :], wgt[:, j % 2, :], ACT.Copy).then_inc(s_whi, 1)

            def v_group(it, last):
                for j in range(8):
                    if not (last and j >= 6):
                        if j < 2:
                            act.wait_ge(s_tile, it * 8 + SPLIT0["v"] + j - 1)
                        w_high(it * 8 + j + 2, j + 2)
                    if not (last and j >= 4):
                        piece = landed8(act, V_PAIR0, it, j + RING)
                        act.wait_ge(s_tile, it * 8 + SPLIT0["v"] + j + 1)
                        hi(j, piece)

            w_high(0, 0)
            w_high(1, 1)
            with act.Fori(0, NE // 8 - 1) as it:
                v_group(it, False)
            v_group(NE // 8 - 1, True)
            act.wait_ge(s_ysum, 1)
            for kc in range(0, KC, 2):
                ch.link(act.activation(y_f[:, kc, :], bank[kc][:, :], ACT.Copy, scale=Y_UNSCALE))
                if kc == 0:
                    act.sem_inc(s_fin0, 1)
            for kc in range(KC):
                if kc % 2:
                    act.wait_ge(s_fin, kc // 2 + 1)
                square(4 * KC + kc, y_f[:, kc, :])
            root(11, 5 * KC - 1, bank[0][:, :], D)

        @block.vector
        def _(dve):
            ch = Chain(dve, s_dve)

            def lo(s, ring, piece):
                dve.wait_ge(s_hi, s + 1)
                dve.scalar_tensor_tensor(out=w_lo[:, ring, :, :].rearrange("p a b -> p (a b)"), in0=piece,
                                         scalar=W_SCALE, in1=w_hi[:, ring, :, :].rearrange("p a b -> p (a b)"),
                                         op0=ALU.mult, op1=ALU.subtract).then_inc(s_lo, 1)

            def lo_at(s):
                if s < SPLIT0["wq"]:
                    kind = "win" if s < SPLIT0["wout"] else "wout"
                    piece = landed(dve, kind, s - SPLIT0[kind])
                else:
                    piece = landed8(dve, WQ_PAIR0, 0, s - SPLIT0["wq"])
                lo(s, s % RING, piece)

            def act_lo_of(m):
                dve.wait_ge(s_acthi, m + 1)
                dve.tensor_tensor(act_lo[:, m % KC, :], tmp[:, m % 2, :], act_hi[:, m % KC, :], ALU.subtract
                                  ).then_inc(s_actlo, 1)

            def invert(r):
                dve.wait_ge(s_root, r + 1)
                dve.reciprocal(rstd[:, r % 2, :], rstd[:, r % 2, :]).then_inc(s_rstd, 1)
                dve.wait_ge(s_rstd, r + 1)

            def norm_rows(which, r, part):
                for kc in range(KC + 1):
                    if kc < KC:
                        if kc >= 2:
                            dve.wait_ge(s_actlo, KC * part + kc - 1)
                        ins = dve.tensor_tensor(tmp[:, kc % 2, :], x_sb[:, kc, :], rstd[:, r % 2, :], ALU.mult)
                        ins.then_inc(s_xr, 1)
                        if kc == KC - 1:
                            dve.wait_ge(s_xr, KC * (which + 1))
                            dve.sem_inc(s_rused, 1)
                    if kc:
                        act_lo_of(KC * part + kc - 1)

            for r in range(2):
                dve.sem_inc(s_psr[r], PRIMED)
                dve.sem_inc(s_oha[r], PRIMED)
            dve.wait_ge(s_par, 16)
            dve.wait_ge(s_ada, 16)
            ch.link(dve.tensor_tensor(mod[:, 0:16], bank[7][:, 0:16], par_sb[:, PB:PB + 16], ALU.add))
            dve.scalar_tensor_tensor(out=amul[:, 0, :], in0=mod[:, SC1:SC1 + 8], scalar=1.0,
                                     in1=par_sb[:, PG1:PG1 + 8], op0=ALU.add, op1=ALU.mult).then_inc(s_mod, 1)
            dve.wait_ge(s_x, 16)
            invert(0)
            norm_rows(0, 0, 0)
            for s in range(RING):
                lo_at(s)
            for i in range(12):
                lo_at(i + RING)
                if i >= 9:
                    dve.wait_ge(s_vtr, i - 8)
                    dve.tensor_copy(v_tok[:, :, P * (i - 9):P * (i - 8)],
                                    bank[4 + (i - 9) % 2][:, :].rearrange("p (a b) -> p a b", a=TT)
                                    ).then_inc(s_vtok, 1)
            dve.wait_ge(s_vtr, 4)
            dve.tensor_copy(v_tok[:, :, 3 * P:4 * P], bank[5][:, :].rearrange("p (a b) -> p a b", a=TT)
                            ).then_inc(s_vtok, 1)
            dve.wait_ge(s_const, 1)
            for k in range(36):
                n, b = k, k % 2
                w = P * (n % TT + 1)
                if k < UNITS:
                    dve.wait_ge(s_score, n + 1)
                    if n >= 2:
                        dve.wait_ge(s_exp, n - 1)
                    dve.tensor_reduce(negmax[:, b:b + 1], bank[2 + b][:, 0:w], AX.X, ALU.max,
                                      negate=True).then_inc(s_nmax, 1)
                if k % 3 == 2:
                    i = 12 + k // 3
                    src = bank[i % 2][:, :]
                    j = i % 4
                    if 16 <= i < 20:
                        dve.wait_ge(s_tile, i + 1)
                        dve.wait_ge(s_evac[j % 2], 7 + j // 2)
                        dve.scalar_tensor_tensor(out=conv_in[:, j, 2:T + 2], in0=src, scalar=UNSCALE,
                                                 in1=gcT[:, j, :], op0=ALU.mult, op1=ALU.mult
                                                 ).then_inc(s_evac[i % 2], 1)
                        dve.wait_ge(s_evac[i % 2], i // 2 + 1)
                        tap = [par_sb[:, PCW + 3 * j + t:PCW + 3 * j + t + 1] for t in range(3)]
                        ch.link(dve.tensor_scalar(y_sb[:, j, :], conv_in[:, j, 0:T], tap[0], None, ALU.mult))
                        for t in (1, 2):
                            ch.link(dve.scalar_tensor_tensor(out=y_sb[:, j, :], in0=conv_in[:, j, t:T + t],
                                                             scalar=tap[t], in1=y_sb[:, j, :],
                                                             op0=ALU.mult, op1=ALU.add))
                    if i >= 20:
                        dve.wait_ge(s_tile, i + 1)
                        dve.scalar_tensor_tensor(out=y_sb[:, j, :], in0=src, scalar=UNSCALE, in1=y_sb[:, j, :],
                                                 op0=ALU.mult, op1=ALU.mult).then_inc(s_evac[i % 2], 1)
                    lo_at(i + RING)
                if k < UNITS:
                    dve.wait_ge(s_exp, n + 1)
                    if n >= 2:
                        dve.wait_ge(s_norm, n - 1)
                    ch.link(dve.reciprocal(rrow[:, b:b + 1], psum_row[:, b:b + 1]))
                    dve.tensor_scalar(probs[:, b, 0:w], probs[:, b, 0:w], rrow[:, b:b + 1], None, ALU.mult
                                      ).then_inc(s_norm, 1)
            for b in range(2):
                dve.wait_ge(s_evac[b], 12)
            dve.sem_inc(s_yc, 4)
            dve.wait_ge(s_ada, 40)
            ch.link(dve.tensor_tensor(mod[:, 16:40], bank[7][:, 16:40], par_sb[:, PB + 16:PB + 40], ALU.add))
            ch.link(dve.tensor_tensor(gmul[:, 0, :], mod[:, GT1:GT1 + 8], par_sb[:, PG1P:PG1P + 8], ALU.mult))
            dve.scalar_tensor_tensor(out=amul[:, 1, :], in0=mod[:, SC2:SC2 + 8], scalar=1.0,
                                     in1=par_sb[:, PG2:PG2 + 8], op0=ALU.add, op1=ALU.mult).then_inc(s_mod, 1)
            for j in range(KC):
                invert(1 + j)
                dve.wait_ge(s_actlo, KC + j - 1)
                dve.scalar_tensor_tensor(out=tmp[:, j % 2, :], in0=y_sb[:, j, :],
                                         scalar=par_sb[:, PGG + j:PGG + j + 1], in1=rstd[:, (1 + j) % 2, :],
                                         op0=ALU.mult, op1=ALU.mult).then_inc(s_act32, 1)
                dve.wait_ge(s_act32, KC + j + 1)
                dve.sem_inc(s_rused, 1)
                act_lo_of(KC + j)
            for i in range(KC):
                lo_at(24 + i + RING)
            dve.wait_ge(s_ada, 48)
            ch.link(dve.tensor_tensor(mod[:, 40:48], bank[4][:, 0:8], par_sb[:, PB + 40:PB + 48], ALU.add))
            ch.link(dve.tensor_tensor(gmul[:, 1, :], mod[:, GT2:GT2 + 8], par_sb[:, PG2P:PG2P + 8], ALU.mult))

            invert(9)
            dve.wait_ge(s_actlo, 2 * KC)
            for kc in range(KC):
                if kc >= 2:
                    dve.wait_ge(s_x1, kc - 1)
                ch.link(dve.scalar_tensor_tensor(out=tmp[:, kc % 2, :], in0=y_sb[:, kc, :],
                                                 scalar=gmul[:, 0, kc:kc + 1], in1=rstd[:, 1, :],
                                                 op0=ALU.mult, op1=ALU.mult))
                dve.tensor_tensor(x_sb[:, kc, :], x_sb[:, kc, :], tmp[:, kc % 2, :], ALU.add).then_inc(s_x1, 1)
            dve.wait_ge(s_x1, KC)
            dve.sem_inc(s_rused, 1)
            invert(10)
            norm_rows(1, 10, 2)

            def top16(n, vals, idx, srcs, works):
                apart(dve)
                for q in range(n):
                    ins = dve.max(vals[q][:, 0:8], srcs[q])
                ch.link(ins)
                apart(dve)
                for q in range(n):
                    dve.max_index(idx[q][:, 0:8], vals[q][:, 0:8], srcs[q])
                for q in range(n):
                    ins = dve.match_replace(out=works[q], in_to_replace=vals[q][:, 0:8], in_values=srcs[q],
                                            imm_value=-3.0e38)
                ch.link(ins)
                apart(dve)
                for q in range(n):
                    ins = dve.max(vals[q][:, 8:16], works[q])
                ch.link(ins)
                apart(dve)
                for q in range(n):
                    ins = dve.max_index(idx[q][:, 8:16], vals[q][:, 8:16], works[q])
                ch.link(ins)

            steps = 8 * 5
            with dve.Fori(0, 2) as it:
                ch.enter(it, steps)
                for j in range(8):
                    lo(it * 8 + 32 + j + RING, j % RING, landed8(dve, WQ_PAIR0, it, j + RING))
                    dve.wait_ge(s_ps[j % 2], it * 4 + j // 2 + 1 + PRIMED)
                    src = bank[2 + j % 2]
                    top16(TT, [top_v[:, q, :] for q in range(TT)], [top_i[:, q, :] for q in range(TT)],
                          [src[:, NK * q:NK * q + NK] for q in range(TT)], [work1[:, q, :] for q in range(TT)])
                    dve.sem_inc(s_psr[j % 2], 1)
                    dve.tensor_copy(all_v[:, :, bass.ds(it * 8 + j, 1), :].rearrange("p t h k -> p t (h k)"),
                                    top_v[:, :, :])
                    ch.link(dve.tensor_copy(
                        all_i[:, :, bass.ds(it * 8 + j, 1), :].rearrange("p t h k -> p t (h k)"), top_i[:, :, :]))
            ch.leave(steps, 2)

            rows = all_v[:, :, :, :].rearrange("p t h k -> p (t h) k")

            def unit(it, j):
                r = j % 2
                ch.link(dve.tensor_tensor(
                    cand[:, :].rearrange("p (a b) -> p a b", a=K16),
                    rows[:, bass.ds(it * 16 + 2 * j, 1), :].rearrange("p a k -> p k a").to_broadcast([P, K16, K16]),
                    rows[:, bass.ds(it * 16 + 2 * j + 1, 1), :].to_broadcast([P, K16, K16]), ALU.add))
                top16(1, [best_v], [best_p], [cand[:, :]], [cand2[:, :]])
                dve.tensor_copy(sel_v[:, bass.ds(it * 128 + K16 * j, K16)], best_v[:, :])
                dve.tensor_scalar(rank[:, r, 0, :], best_p[:, :], 4, None, ALU.logical_shift_right)
                ch.link(dve.tensor_scalar(rank[:, r, 1, :], best_p[:, :], 15, None, ALU.bitwise_and))
                dve.tensor_tensor(onehot16[:, r, :, :].rearrange("p h (k a) -> p (h k) a", a=K16),
                                  rank[:, r, :, :].rearrange("p h k -> p (h k)").unsqueeze(2)
                                  .to_broadcast([P, 2 * K16, K16]),
                                  iota16[:, :].unsqueeze(1).to_broadcast([P, 2 * K16, K16]),
                                  ALU.is_equal).then_inc(s_rank, 1)

            def unit_sum(it, j):
                r = j % 2
                dve.wait_ge(s_oh, it * 8 + j + 1)
                dve.tensor_reduce(sel_i[:, :, bass.ds(it * 128 + K16 * j, K16)],
                                  onehot16[:, r, :, :].rearrange("p h (k a) -> p h k a", k=K16), AX.X, ALU.add
                                  ).then_inc(s_seli, 1)

            steps = 8 * 6
            with dve.Fori(0, UNITS // 8) as it:
                ch.enter(it, steps)
                for j in range(8):
                    unit(it, j)
                    lo(it * 8 + SPLIT0["u"] + j + RING, j % RING, landed8(dve, U_PAIR0, it, j + RING))
                    if j:
                        unit_sum(it, j - 1)
                unit_sum(it, 7)
            ch.leave(steps, UNITS // 8)

            sv = sel_v[:, :].rearrange("p (u k) -> p u k", k=K16)
            ch.link(dve.tensor_copy(sel_sum[:, :].unsqueeze(2), sv[:, :, 0:1]))
            dve.tensor_tensor(sv, sv, sel_sum[:, :].unsqueeze(2).to_broadcast([P, UNITS, K16]), ALU.subtract
                              ).then_inc(s_selv, 1)
            g = UNITS // 8
            for j in range(8):
                if j == 1:
                    dve.wait_ge(s_selexp, 1)
                    ch.link(dve.tensor_reduce(sel_sum[:, :], sv, AX.X, ALU.add))
                    ch.link(dve.reciprocal(sel_sum[:, :], sel_sum[:, :]))
                    dve.scalar_tensor_tensor(out=sv, in0=sv, scalar=G_SCALE,
                                             in1=sel_sum[:, :].unsqueeze(2).to_broadcast([P, UNITS, K16]),
                                             op0=ALU.mult, op1=ALU.mult).then_inc(s_gate, 1)
                lo(g * 8 + SPLIT0["u"] + j + RING, j % RING, landed8(dve, U_PAIR0, g, j + RING))
                if j == 5:
                    dve.wait_ge(s_gtr, 1)
                    dve.tensor_copy(idxT[:, 0, :], bank[2][:, :])
                    dve.tensor_copy(idxT[:, 1, :], bank[3][:, :])
                    ch.link(dve.tensor_copy(gateT[:, :], bank[4][:, :]))
                    ch.link(dve.tensor_copy(gate16[:, :], gateT[:, :]))
                    dve.tensor_copy(idxT[:, 2, :], gate16[:, :])
                    dve.tensor_tensor(idxT[:, 3, :], gateT[:, :], gate16[:, :], ALU.subtract).then_inc(s_idx, 1)

            with dve.Fori(0, GCH // 8) as it:
                for j in range(8):
                    r = j % 2
                    dve.wait_ge(s_scal, it * 8 + j + 1)
                    dve.wait_ge(s_gb[r], it * 8 + 2 * (j // 2) + PRIMED)
                    for t in range(GTOK):
                        for q, rows_ in ((2, oh_h), (3, oh_l)):
                            ins = dve.tensor_scalar(rows_[:, r, t, :], iota_f[:, :], scal[:, r, 0, t:t + 1],
                                                    scal[:, r, q, t:t + 1], ALU.is_equal, ALU.mult)
                    ins.then_inc(s_oha[r], 1)
                    lo(it * 8 + SPLIT0["u"] + G0 + j + RING, j % RING,
                       landed8(dve, U_PAIR0 + G0 // 2, it, j + RING))
            with dve.Fori((G0 + GCH) // 8, NE // 8) as it:
                for j in range(8):
                    lo(it * 8 + SPLIT0["u"] + j + RING, j % RING, landed8(dve, U_PAIR0, it, j + RING))

            def weigh(c, it, j):
                dve.wait_ge(s_agin[j % 4], it * 64 + 32 * (j // 4 + 1))
                if j >= 2:
                    dve.wait_ge(s_wlo, c - 1)
                dve.tensor_tensor(wgt[:, j % 2, :], a_in[:, j % 4, :], g_in[:, j % 4, :], ALU.mult
                                  ).then_inc(s_w32, 1)
                dve.wait_ge(s_whi, c + 1)
                dve.tensor_tensor(wgt_lo[:, j % 4, :], wgt[:, j % 2, :], wgt_hi[:, j % 4, :], ALU.subtract
                                  ).then_inc(s_wlo, 1)

            def v_group(it, last):
                for j in range(8):
                    if not (last and j >= 6):
                        weigh(it * 8 + j + 2, it, j + 2)
                    if not (last and j >= 4):
                        lo(it * 8 + SPLIT0["v"] + j + RING, j % RING, landed8(dve, V_PAIR0, it, j + RING))

            weigh(0, 0, 0)
            weigh(1, 0, 1)
            with dve.Fori(0, NE // 8 - 1) as it:
                v_group(it, False)
            v_group(NE // 8 - 1, True)
            dve.wait_ge(s_ysum, 1)
            for kc in range(1, KC, 2):
                dve.tensor_scalar(y_f[:, kc, :], bank[kc][:, :], Y_UNSCALE, None, ALU.mult).then_inc(s_fin, 1)
            invert(11)
            for kc in range(KC):
                if kc >= 2:
                    dve.wait_ge(s_fin2, kc - 1)
                ch.link(dve.scalar_tensor_tensor(out=tmp[:, kc % 2, :], in0=y_f[:, kc, :],
                                                 scalar=gmul[:, 1, kc:kc + 1], in1=rstd[:, 1, :],
                                                 op0=ALU.mult, op1=ALU.mult))
                dve.tensor_tensor(y_f[:, kc, :], x_sb[:, kc, :], tmp[:, kc % 2, :], ALU.add).then_inc(s_fin2, 1)

        @block.tensor
        def _(pe):
            def ada_chunk(i):
                w = landed(pe, "ada", i)
                dst, col = (bank[7], i) if i < 40 else (bank[4], i - 40)
                for kc in range(KC):
                    ins = pe.matmul(dst[:, col:col + 1], w[:, P * kc:P * kc + P], silu_c[:, kc:kc + 1],
                                    start=(kc == 0), stop=(kc == KC - 1))
                ins.then_inc(s_ada, 1)

            def stat(m, kc, n, lhs, dst):
                pe.wait_ge(s_sq, m + 1)
                pe.matmul(dst[:, :], lhs[:, :], sq[:, m % 2, :], start=(kc == 0), stop=(kc == n - 1)
                          ).then_inc(s_stat, 1)

            def part(s, ring, p, dst):
                if p == 0:
                    pe.wait_ge(s_hi, s + 1)
                if p == 2:
                    pe.wait_ge(s_lo, s + 1)
                w = w_lo if p == 2 else w_hi
                a = act_lo if p == 1 else act_hi
                for kc in range(KC):
                    ins = pe.matmul(dst[:, :], w[:, ring, kc, :], a[:, kc, :], start=(p == 0 and kc == 0),
                                    stop=(p == 2 and kc == KC - 1))
                if p == 2:
                    ins.then_inc(s_tile, 1)

            def tile(s, ring, dst):
                for p in range(3):
                    part(s, ring, p, dst)

            def tile_at(s):
                pe.wait_ge(s_evac[s % 2], s // 2)
                tile(s, s % RING, bank[s % 2])

            for r in range(2):
                pe.sem_inc(s_ps[r], PRIMED)
                pe.sem_inc(s_gb[r], PRIMED)
            pe.wait_ge(s_silu, 1)
            for i in range(8):
                ada_chunk(i)
            pe.wait_ge(s_const, 1)
            for kc in range(KC):
                stat(kc, kc, KC, ones, bank[6])
            for i in range(8, 16):
                ada_chunk(i)
            pe.wait_ge(s_acthi, KC)
            pe.wait_ge(s_actlo, KC)

            def v_transpose(j):
                pe.wait_ge(s_evac[j % 2], 4 + j // 2 + 1)
                if j >= 2:
                    pe.wait_ge(s_vtok, j - 1)
                for kt in range(TT):
                    ins = pe.transpose(bank[4 + j % 2][:, P * kt:P * kt + P], vT[:, j % 2, P * kt:P * kt + P],
                                       ident[:, :])
                ins.then_inc(s_vtr, 1)

            for i in range(12):
                tile_at(i)
                if i >= 9:
                    v_transpose(i - 9)
                if i % 2:
                    ada_chunk(16 + i - 1)
                    ada_chunk(16 + i)

            def scores(n):
                h, qt, b = 2 * (n // 8) + n % 8 // 4, n % 4, n % 2
                r0 = HD * (h % 2)
                if n >= 2:
                    pe.wait_ge(s_exp, n - 1)
                dst = bank[2 + b]
                pe.matmul(dst[:, 0:P * (qt + 1)], qT[r0:r0 + HD, h // 2, P * qt:P * qt + P],
                          kT[r0:r0 + HD, h // 2, 0:P * (qt + 1)], start=True, stop=False)
                pe.matmul(dst[:, P * qt:P * qt + P], ident_bf[:, :], mask_bf[:, :], start=False, stop=True
                          ).then_inc(s_score, 1)

            def transposes(n):
                qt, b = n % 4, n % 2
                pe.wait_ge(s_norm, n + 1)
                if n >= 2:
                    pe.wait_ge(s_pT, n - 1)
                for kt in range(qt + 1):
                    ins = pe.transpose(bank[4 + b][:, P * kt:P * kt + P], probs[:, b, P * kt:P * kt + P],
                                       ident[:, :])
                ins.then_inc(s_ptr, 1)

            def values(n):
                h, qt, b = 2 * (n // 8) + n % 8 // 4, n % 4, n % 2
                r0 = HD * (h % 2)
                pe.wait_ge(s_pT, n + 1)
                if n % 8 == 0 and n:
                    pe.wait_ge(s_ya, n // 8)
                for kt in range(qt + 1):
                    ins = pe.matmul(bank[6][r0:r0 + HD, P * qt:P * qt + P], v_tok[:, kt, HD * h:HD * h + HD],
                                    probsT[:, b, P * kt:P * kt + P], start=(kt == 0), stop=(kt == qt))
                ins.then_inc(s_pv, 1)

            for k in range(36):
                i = 12 + k // 3
                if k % 3 == 0:
                    pe.wait_ge(s_evac[i % 2], i // 2)
                part(i, i % RING, k % 3, bank[i % 2])
                if k == 0:
                    v_transpose(3)
                if k == 1:
                    pe.wait_ge(s_vtok, 4)
                if k < UNITS:
                    scores(k)
                if 1 <= k <= UNITS:
                    transposes(k - 1)
                if 2 <= k <= UNITS + 1:
                    values(k - 2)
                if k % 6 == 5:
                    ada_chunk(16 + i - 1)
                    ada_chunk(16 + i)
            for j in range(KC):
                if j >= 2:
                    pe.wait_ge(s_root, j)
                stat(KC + j, 0, 1, group_ones, bank[2 + j % 2])
            pe.wait_ge(s_acthi, 2 * KC)
            pe.wait_ge(s_actlo, 2 * KC)
            for i in range(KC):
                tile_at(24 + i)
                if i:
                    stat(2 * KC + i - 1, i - 1, KC, ones, bank[5])
                if i % 2:
                    ada_chunk(40 + i - 1)
                    ada_chunk(40 + i)
            stat(3 * KC - 1, KC - 1, KC, ones, bank[5])
            for kc in range(KC):
                stat(3 * KC + kc, kc, KC, ones, bank[6])
            pe.wait_ge(s_acthi, 3 * KC)
            pe.wait_ge(s_actlo, 3 * KC)
            pe.wait_ge(s_keys, 16)
            for b in range(2):
                pe.wait_ge(s_evac[b], 16)

            def peer_scores(it, j):
                pe.wait_ge(s_evac[j % 2], it * 4 + 16 + j // 2 + 1)
                pe.wait_ge(s_psr[j % 2], it * 4 + j // 2 + PRIMED)
                for tt in range(TT):
                    ins = pe.matmul(bank[2 + j % 2][:, NK * tt:NK * tt + NK], pq[:, j % 2, P * tt:P * tt + P],
                                    keys_sb[:, bass.ds(it * 8 + j, 1), :].rearrange("p a n -> p (a n)"),
                                    start=True, stop=True)
                ins.then_inc(s_ps[j % 2], 1)

            with pe.Fori(0, 2) as it:
                for j in range(8):
                    pe.wait_ge(s_evac[j % 2], it * 4 + 16 + j // 2)
                    tile(it * 8 + 32 + j, j % RING, bank[j % 2])
                    if j:
                        peer_scores(it, j - 1)
                peer_scores(it, 7)
            for b in range(2):
                pe.wait_ge(s_evac[b], 24)

            def expert_tile(it, j):
                if j >= 2:
                    pe.wait_ge(s_gelu, it * 8 + j - 1)
                else:
                    pe.wait_ge(s_hi, it * 8 + SPLIT0["u"] + j + 3)
                tile(it * 8 + SPLIT0["u"] + j, j % RING, bank[j % 2])

            with pe.Fori(0, UNITS // 8) as it:
                for j in range(8):
                    expert_tile(it, j)
            for j in range(8):
                expert_tile(UNITS // 8, j)
                if j == 2:
                    pe.wait_ge(s_gate, 1)
                    pe.wait_ge(s_seli, UNITS)
                    for q, src in enumerate((sel_i[:, 0, :], sel_i[:, 1, :], sel_v[:, :])):
                        for tt in range(TT):
                            ins = pe.transpose(bank[2 + q][:, P * tt:P * tt + P], src[:, P * tt:P * tt + P],
                                               ident[:, :])
                    ins.then_inc(s_gtr, 1)

            def spread(it, j):
                r = j % 2
                pe.wait_ge(s_ohb, it * 8 + j + 1)
                pe.wait_ge(s_oha[r], it * 4 + j // 2 + 1 + PRIMED)
                pe.wait_ge(s_gev[r], it * 8 + 2 * (j // 2) + PRIMED)
                for q in range(2):
                    dst = bank[2 + 2 * r + q]
                    for t in range(4):
                        tok = 4 * q + t
                        pe.matmul(dst[:, P * t:P * t + P], oh_b[:, r, tok, :], oh_h[:, r, tok, :],
                                  start=True, stop=False)
                        ins = pe.matmul(dst[:, P * t:P * t + P], oh_b[:, r, tok, :], oh_l[:, r, tok, :],
                                        start=False, stop=True)
                    ins.then_inc(s_gb[r], 1)

            pe.wait_ge(s_idx, 1)
            with pe.Fori(0, GCH // 8) as it:
                for j in range(8):
                    expert_tile(it + G0 // 8, j)
                    spread(it, j)
            with pe.Fori((G0 + GCH) // 8, NE // 8) as it:
                for j in range(8):
                    expert_tile(it, j)

            pe.wait_ge(s_gelu, NE)
            for r in range(2):
                pe.wait_ge(s_gev[r], GCH + PRIMED)
            for dt in range(KC):
                pe.matmul(bank[dt][:, :], zeros16[:, :], act_hi[:, dt, :], start=True, stop=False)

            def v_tile(it, j, last):
                s = it * 8 + SPLIT0["v"] + j
                c = it * 8 + j
                pe.wait_ge(s_hi, s + 1)
                pe.wait_ge(s_lo, s + 1)
                pe.wait_ge(s_whi, c + 1)
                pe.wait_ge(s_wlo, c + 1)
                for dt in range(KC):
                    for w, a in ((w_hi, wgt_hi), (w_hi, wgt_lo), (w_lo, wgt_hi)):
                        ins = pe.matmul(bank[dt][:, :], w[:, j % RING, dt, :], a[:, j % 4, :], start=False,
                                        stop=(last and j == 7 and w is w_lo))
                ins.then_inc(s_tile, 1)
                return ins

            with pe.Fori(0, NE // 8 - 1) as it:
                for j in range(8):
                    v_tile(it, j, False)
            for j in range(8):
                v_tile(NE // 8 - 1, j, True)
            pe.wait_ge(s_tile, SPLIT0["v"] + NE)
            pe.sem_inc(s_ysum, 1)
            pe.wait_ge(s_fin0, 1)
            for kc in range(KC):
                stat(4 * KC + kc, kc, KC, ones, bank[0])


def tiles(w):
    k, n = w.shape
    return np.ascontiguousarray(w.reshape(k // P, P, n // P, P).transpose(2, 1, 0, 3)).reshape(n // P, P, k)


def columns(vec):
    return vec.reshape(-1, P).T


def kernel(**inputs):
    import concourse.bacc as bacc
    from concourse.bass_utils import run_bass_kernel_spmd as run

    i = {k: np.asarray(a) for k, a in inputs.items()}
    conv = i["conv_w"][0].reshape(3, NCONV, P).transpose(2, 1, 0).reshape(P, 3 * NCONV)
    arrays = {
        "xT": np.ascontiguousarray(i["x"][0].T.reshape(KC, P, T).transpose(1, 0, 2)),
        "par": np.ascontiguousarray(np.concatenate([
            columns(i["mix_pre_gain"][0]), columns(i["mix_post_gain"][0]), columns(i["group_gain"][0]),
            columns(i["ffn_pre_gain"][0]), columns(i["ffn_post_gain"][0]), columns(i["c"][0]),
            columns(i["ada_b"][0]), conv], axis=1)),
        "ada": tiles(i["ada_w"][0]),
        "win": tiles(i["w_in"][0]),
        "wout": tiles(i["w_out"][0]),
        "wq": tiles(i["peer_wq"][0]),
        "keys": np.ascontiguousarray(i["peer_keys"][0].reshape(2 * PH, NK, P).transpose(2, 0, 1)),
        "u": np.ascontiguousarray(i["peer_u"][0].reshape(NE, P, KC, P).transpose(0, 3, 2, 1)).reshape(NE, P, D),
        "v": np.ascontiguousarray(i["peer_v"][0].reshape(NE, P, D)),
    }
    nc = bacc.Bacc("TRN2", target_bir_lowering=False, num_devices=1)
    args = [nc.dram_tensor(name, a.shape, mybir.dt.from_np(a.dtype), kind="ExternalInput").ap()
            for name, a in arrays.items()]
    out = nc.dram_tensor("outT", (P, KC, T), F32, kind="ExternalOutput").ap()
    build(nc, *args, out)
    r = run(nc, [arrays], core_ids=[0])
    o = r.results[0]["outT"]
    return np.ascontiguousarray(o.transpose(1, 0, 2).reshape(D, T).T).reshape(1, T, D)
```
